# Optimizing a Trainium2 kernel written in Bass

```python
import jax, jax.numpy as jnp
from jax import lax
import numpy as np

D_MODEL = 1024
BATCH = 1
SEQ = 256
DEPTH = 2

GRID_W = 64
CTX_LEN = 256
HEAD_DIM = 64
ROPE_THETA = 10000.0
NORM_EPS = 1e-6
Q_BLOCK = 128

A_HEADS = 8
A_KV_HEADS = 2
A_Q_W = A_HEADS * HEAD_DIM
A_KV_W = A_KV_HEADS * HEAD_DIM
B_HEADS = 8
B_Q_LORA = 384
B_KV_LORA = 256
B_NOPE = 64
B_ROPE = 32
B_V = 64
C_HEADS = 8
C_W = C_HEADS * HEAD_DIM
C_DECAY_LORA = 64
C_AAA_LORA = 64
C_GATE_LORA = 128
C_GN_EPS = 64e-5
D_HEADS = 8
D_W = D_HEADS * HEAD_DIM
NA_ROWS = 8
NA_COLS = 16

N_BRANCH = 4
BRANCH_W = 512
D_FF = 4 * D_MODEL

A_IN = A_Q_W + 2 * A_KV_W
B_IN = B_Q_LORA + B_KV_LORA + B_ROPE
C_IN = 3 * C_W + 2 * C_DECAY_LORA + 2 * C_AAA_LORA + C_GATE_LORA
D_IN = 3 * D_W
GATE_IN = N_BRANCH * D_MODEL
N_IN = A_IN + B_IN + C_IN + D_IN + GATE_IN

kernel_name = 'hybrid_prefix_flow_block'

def _split(p, widths):
    cuts = [int(v) for v in np.cumsum(widths)[:-1]]
    return jnp.split(p, cuts, axis=-1)

def rms_norm(x, g):
    xf = x.astype(jnp.float32)
    y = xf * lax.rsqrt(jnp.mean(xf * xf, axis=-1, keepdims=True) + NORM_EPS)
    return (y * g.astype(jnp.float32)).astype(x.dtype)

def modulate(h, shift, scale):
    return h * (1 + scale) + shift

def _rope_1d(x, pos):
    half = x.shape[-1] // 2
    inv = ROPE_THETA ** (-jnp.arange(half, dtype=jnp.float32) / half)
    ang = pos.astype(jnp.float32)[:, None] * inv[None, :]
    cos = jnp.cos(ang)[None, :, None, :]
    sin = jnp.sin(ang)[None, :, None, :]
    xf = x.astype(jnp.float32)
    x1, x2 = xf[..., :half], xf[..., half:]
    return jnp.concatenate([x1 * cos - x2 * sin, x1 * sin + x2 * cos], -1).astype(x.dtype)

def rope_2d(x, rows, cols):
    h = x.shape[-1] // 2
    return jnp.concatenate([_rope_1d(x[..., :h], rows), _rope_1d(x[..., h:], cols)], -1)

def block_attention(q, k, v):
    b, tq, hk, g, d = q.shape
    nb = tq // Q_BLOCK
    kf = k.astype(jnp.float32)
    vf = v.astype(jnp.float32)
    qb = jnp.moveaxis(q.reshape(b, nb, Q_BLOCK, hk, g, d), 1, 0)
    scale = d ** -0.5

    def one_block(qi):
        s = jnp.einsum('bqkgd,bskd->bkgqs', qi.astype(jnp.float32), kf) * scale
        p = jax.nn.softmax(s, axis=-1)
        return jnp.einsum('bkgqs,bskd->bqkgd', p, vf)

    o = lax.map(one_block, qb)
    return jnp.moveaxis(o, 0, 1).reshape(b, tq, hk * g * v.shape[-1]).astype(q.dtype)

def _gqa_heads(p, q_gain, k_gain, rows, cols):
    b, t, _ = p.shape
    q, k, v = _split(p, (A_Q_W, A_KV_W, A_KV_W))
    q = rms_norm(q.reshape(b, t, A_HEADS, HEAD_DIM), q_gain)
    k = rms_norm(k.reshape(b, t, A_KV_HEADS, HEAD_DIM), k_gain)
    v = v.reshape(b, t, A_KV_HEADS, HEAD_DIM)
    if rows is not None:
        q = rope_2d(q, rows, cols)
        k = rope_2d(k, rows, cols)
    return q.reshape(b, t, A_KV_HEADS, A_HEADS // A_KV_HEADS, HEAD_DIM), k, v

def gqa_mixer(p_lat, p_ctx, q_gain, k_gain, rows, cols, with_ctx):
    ql, kl, vl = _gqa_heads(p_lat, q_gain, k_gain, rows, cols)
    qc, kc, vc = _gqa_heads(p_ctx, q_gain, k_gain, None, None)
    o_lat = block_attention(ql, jnp.concatenate([kc, kl], 1), jnp.concatenate([vc, vl], 1))
    o_ctx = block_attention(qc, kc, vc) if with_ctx else None
    return o_lat, o_ctx

def _mla_heads(p, q_gain, kv_gain, w_q_up, w_kv_up, rows, cols):
    b, t, _ = p.shape
    cq, ckv, kr = _split(p, (B_Q_LORA, B_KV_LORA, B_ROPE))
    q = (rms_norm(cq, q_gain) @ w_q_up).reshape(b, t, B_HEADS, B_NOPE + B_ROPE)
    kv = (rms_norm(ckv, kv_gain) @ w_kv_up).reshape(b, t, B_HEADS, B_NOPE + B_V)
    q_nope, q_rope = q[..., :B_NOPE], q[..., B_NOPE:]
    k_nope, v = kv[..., :B_NOPE], kv[..., B_NOPE:]
    k_rope = kr.reshape(b, t, 1, B_ROPE)
    if rows is not None:
        q_rope = rope_2d(q_rope, rows, cols)
        k_rope = rope_2d(k_rope, rows, cols)
    k = jnp.concatenate([k_nope, jnp.broadcast_to(k_rope, (b, t, B_HEADS, B_ROPE))], -1)
    q = jnp.concatenate([q_nope, q_rope], -1)
    return q[:, :, :, None, :], k, v

def mla_mixer(p_lat, p_ctx, q_gain, kv_gain, w_q_up, w_kv_up, rows, cols, with_ctx):
    ql, kl, vl = _mla_heads(p_lat, q_gain, kv_gain, w_q_up, w_kv_up, rows, cols)
    qc, kc, vc = _mla_heads(p_ctx, q_gain, kv_gain, w_q_up, w_kv_up, None, None)
    o_lat = block_attention(ql, jnp.concatenate([kc, kl], 1), jnp.concatenate([vc, vl], 1))
    o_ctx = block_attention(qc, kc, vc) if with_ctx else None
    return o_lat, o_ctx

def _rwkv_prepare(z, mu, w0, w_decay, a0, w_aaa, w_gate, k_k, k_a):
    f = lambda t: t.astype(jnp.float32)
    b, t, _ = z.shape
    zf = f(z)
    zp = jnp.pad(zf, ((0, 0), (1, 1), (0, 0)))
    zf = zf + (0.5 * (zp[:, :-2] + zp[:, 2:]) - zf) * f(mu)
    r, k, v, w_lo_f, w_lo_b, a_lo_f, a_lo_b, g_lo = _split(
        zf, (C_W, C_W, C_W, C_DECAY_LORA, C_DECAY_LORA, C_AAA_LORA, C_AAA_LORA, C_GATE_LORA))
    heads = lambda u: u.reshape(b, t, C_HEADS, HEAD_DIM)
    kk = heads(k * f(k_k))
    kk = kk / jnp.maximum(jnp.sqrt(jnp.sum(kk * kk, -1, keepdims=True)), 1e-12)
    decays, aas, ks = [], [], []
    for d, (w_lo, a_lo) in enumerate(((w_lo_f, a_lo_f), (w_lo_b, a_lo_b))):
        logw = -jax.nn.softplus(-(f(w0[d]) + jnp.tanh(w_lo) @ f(w_decay[d]))) - 0.5
        decays.append(heads(jnp.exp(-jnp.exp(logw))))
        a = jax.nn.sigmoid(f(a0[d]) + a_lo @ f(w_aaa[d]))
        aas.append(heads(a))
        ks.append(heads(k * (1 + (a - 1) * f(k_a))))
    g = jax.nn.sigmoid(g_lo) @ f(w_gate)
    return heads(r), heads(v), kk, ks, decays, aas, g

def _wkv_scan(r, w, k, v, kk, a, s0, reverse):
    def step(S, inp):
        r_t, w_t, k_t, v_t, kk_t, a_t = inp
        sa = jnp.einsum('bhvk,bhk->bhv', S, kk_t)
        S = (S * w_t[:, :, None, :] - sa[..., None] * (kk_t * a_t)[:, :, None, :]
             + v_t[..., None] * k_t[:, :, None, :])
        return S, jnp.einsum('bhvk,bhk->bhv', S, r_t)
    xs = tuple(jnp.moveaxis(u, 1, 0) for u in (r, w, k, v, kk, a))
    S, ys = lax.scan(step, s0, xs, reverse=reverse)
    return jnp.moveaxis(ys, 0, 1), S

def _rwkv_out(y, r, v, ks, g, r_k, gn_w, gn_b, dtype):
    b, t = y.shape[:2]
    mean = jnp.mean(y, -1, keepdims=True)
    var = jnp.mean(jnp.square(y - mean), -1, keepdims=True)
    yn = ((y - mean) * lax.rsqrt(var + C_GN_EPS)).reshape(b, t, C_W)
    yn = yn * gn_w.astype(jnp.float32) + gn_b.astype(jnp.float32)
    bonus = jnp.sum(r * (ks[0] + ks[1]) * r_k.astype(jnp.float32), -1, keepdims=True) * v
    return ((yn + bonus.reshape(b, t, C_W)) * g).astype(dtype)

def rwkv_mixer(z_lat, z_ctx, mu, w0, w_decay, a0, w_aaa, w_gate, k_k, k_a, r_k, gn_w, gn_b, with_ctx):
    rl, vl, kkl, ksl, wl, al, gl = _rwkv_prepare(z_lat, mu, w0, w_decay, a0, w_aaa, w_gate, k_k, k_a)
    rc, vc, kkc, ksc, wc, ac, gc = _rwkv_prepare(z_ctx, mu, w0, w_decay, a0, w_aaa, w_gate, k_k, k_a)
    s0 = jnp.zeros((z_lat.shape[0], C_HEADS, HEAD_DIM, HEAD_DIM), jnp.float32)
    y_lat, y_ctx = [], []
    for d in range(2):
        rev = d == 1
        yc, s_ctx = _wkv_scan(rc, wc[d], ksc[d], vc, kkc, ac[d], s0, rev)
        yl, _ = _wkv_scan(rl, wl[d], ksl[d], vl, kkl, al[d], s_ctx, rev)
        y_lat.append(yl)
        y_ctx.append(yc)
    o_lat = _rwkv_out(y_lat[0] + y_lat[1], rl, vl, ksl, gl, r_k, gn_w, gn_b, z_lat.dtype)
    o_ctx = _rwkv_out(y_ctx[0] + y_ctx[1], rc, vc, ksc, gc, r_k, gn_w, gn_b, z_ctx.dtype) if with_ctx else None
    return o_lat, o_ctx

def _heads(u, h):
    b, n, _ = u.shape
    return u.reshape(b, n, h, -1)

def nat_mixer(p_lat, p_ctx, rel_bias, with_ctx):
    ql, kl, vl = [_heads(u, D_HEADS) for u in _split(p_lat, (D_W, D_W, D_W))]
    qc, kc, vc = [_heads(u, D_HEADS) for u in _split(p_ctx, (D_W, D_W, D_W))]
    b, s, h, d = ql.shape
    n_rows = s // GRID_W
    kr = min(NA_ROWS, n_rows)
    n_nb = kr * NA_COLS
    scale = d ** -0.5
    kcf, vcf = kc.astype(jnp.float32), vc.astype(jnp.float32)
    qg = jnp.moveaxis(ql.reshape(b, n_rows, GRID_W, h, d), 1, 0)
    kg = kl.astype(jnp.float32).reshape(b, n_rows, GRID_W, h, d)
    vg = vl.astype(jnp.float32).reshape(b, n_rows, GRID_W, h, d)
    col = jnp.arange(GRID_W)
    col_idx = jnp.clip(col - NA_COLS // 2, 0, GRID_W - NA_COLS)[:, None] + jnp.arange(NA_COLS)[None, :]
    dcol = col_idx - col[:, None] + (NA_COLS - 1)

    def one_row(args):
        r, q_r = args
        q_r = q_r.astype(jnp.float32)
        r0 = jnp.clip(r - kr // 2, 0, n_rows - kr)
        k_nb = lax.dynamic_slice_in_dim(kg, r0, kr, axis=1)[:, :, col_idx]
        v_nb = lax.dynamic_slice_in_dim(vg, r0, kr, axis=1)[:, :, col_idx]
        drow = r0 + jnp.arange(kr) - r + (NA_ROWS - 1)
        bias = rel_bias[:, drow[None, :, None], dcol[:, None, :]].astype(jnp.float32)
        s_nb = (jnp.einsum('bqhd,brqjhd->bhqrj', q_r, k_nb) * scale + bias[None]).reshape(b, h, GRID_W, n_nb)
        s_cx = jnp.einsum('bqhd,bchd->bhqc', q_r, kcf) * scale
        pr = jax.nn.softmax(jnp.concatenate([s_nb, s_cx], -1), axis=-1)
        p_nb = pr[..., :n_nb].reshape(b, h, GRID_W, kr, NA_COLS)
        return (jnp.einsum('bhqrj,brqjhd->bqhd', p_nb, v_nb)
                + jnp.einsum('bhqc,bchd->bqhd', pr[..., n_nb:], vcf))

    o = lax.map(one_row, (jnp.arange(n_rows), qg))
    o_lat = jnp.moveaxis(o, 0, 1).reshape(b, s, h * d).astype(p_lat.dtype)
    o_ctx = block_attention(qc[:, :, :, None, :], kc, vc) if with_ctx else None
    return o_lat, o_ctx

def _merge(outs, gate_logits, w_branch, w_out):
    b, t, _ = gate_logits.shape
    gates = jax.nn.sigmoid(gate_logits).reshape(b, t, N_BRANCH, D_MODEL)
    y = gates[:, :, 0] * (outs[0] @ w_branch[0])
    for i in range(1, N_BRANCH):
        y = y + gates[:, :, i] * (outs[i] @ w_branch[i])
    return y @ w_out

def _mlp(h, w1, w2):
    return jnp.square(jax.nn.relu(h @ w1)) @ w2

def _layer(x, xc, rows, cols, mod_lat, mod_ctx, lp, last):
    sh1, sc1, gt1, sh2, sc2, gt2 = jnp.split(mod_lat, 6, axis=-1)
    csh1, csc1, cgt1, csh2, csc2, cgt2 = jnp.split(mod_ctx, 6, axis=-1)
    with_ctx = not last
    p_l = modulate(rms_norm(x, lp['g_norm1']), sh1, sc1) @ lp['w_in']
    p_c = modulate(rms_norm(xc, lp['g_norm1']), csh1, csc1) @ lp['w_in']
    a_l, b_l, c_l, d_l, g_l = _split(p_l, (A_IN, B_IN, C_IN, D_IN, GATE_IN))
    a_c, b_c, c_c, d_c, g_c = _split(p_c, (A_IN, B_IN, C_IN, D_IN, GATE_IN))
    oa = gqa_mixer(a_l, a_c, lp['a_q_gain'], lp['a_k_gain'], rows, cols, with_ctx)
    ob = mla_mixer(b_l, b_c, lp['b_q_gain'], lp['b_kv_gain'], lp['b_w_q_up'], lp['b_w_kv_up'], rows, cols, with_ctx)
    oc = rwkv_mixer(c_l, c_c, lp['c_mu'], lp['c_w0'], lp['c_w_decay'], lp['c_a0'], lp['c_w_aaa'], lp['c_w_gate'],
                    lp['c_k_k'], lp['c_k_a'], lp['c_r_k'], lp['c_gn_w'], lp['c_gn_b'], with_ctx)
    od = nat_mixer(d_l, d_c, lp['d_rel_bias'], with_ctx)
    x = x + gt1 * _merge((oa[0], ob[0], oc[0], od[0]), g_l, lp['w_branch'], lp['w_out'])
    x = x + gt2 * _mlp(modulate(rms_norm(x, lp['g_norm2']), sh2, sc2), lp['w_mlp1'], lp['w_mlp2'])
    if last:
        return x, None
    xc = xc + cgt1 * _merge((oa[1], ob[1], oc[1], od[1]), g_c, lp['w_branch'], lp['w_out'])
    xc = xc + cgt2 * _mlp(modulate(rms_norm(xc, lp['g_norm2']), csh2, csc2), lp['w_mlp1'], lp['w_mlp2'])
    return x, xc

def setup_inputs(seed: int = 0) -> dict:
    key = jax.random.key(seed)
    keys = iter(jax.random.split(key, 48))
    L, D = DEPTH, D_MODEL

    def nrm(shape, std):
        return std * jax.random.normal(next(keys), shape, jnp.float32)

    def gain(shape):
        return 1.0 + 0.05 * jax.random.normal(next(keys), shape, jnp.float32)

    return {
        'x': nrm((BATCH, SEQ, D), 1.0),
        'c': nrm((BATCH, D), 1.0),
        'ctx': nrm((BATCH, CTX_LEN, D), 1.0),
        'c_ctx': nrm((D,), 1.0),
        'w_ada': nrm((L, D, 6 * D), 0.5 * D ** -0.5),
        'b_ada': nrm((L, 6 * D), 0.02),
        'g_norm1': gain((L, D)),
        'g_norm2': gain((L, D)),
        'w_in': nrm((L, D, N_IN), D ** -0.5),
        'a_q_gain': gain((L, HEAD_DIM)),
        'a_k_gain': gain((L, HEAD_DIM)),
        'b_q_gain': gain((L, B_Q_LORA)),
        'b_kv_gain': gain((L, B_KV_LORA)),
        'b_w_q_up': nrm((L, B_Q_LORA, B_HEADS * (B_NOPE + B_ROPE)), B_Q_LORA ** -0.5),
        'b_w_kv_up': nrm((L, B_KV_LORA, B_HEADS * (B_NOPE + B_V)), B_KV_LORA ** -0.5),
        'c_mu': jax.random.uniform(next(keys), (L, C_IN), jnp.float32),
        'c_w0': jax.random.uniform(next(keys), (L, 2, C_W), jnp.float32, minval=-6.0, maxval=-1.0),
        'c_w_decay': nrm((L, 2, C_DECAY_LORA, C_W), 0.1),
        'c_a0': nrm((L, 2, C_W), 0.5),
        'c_w_aaa': nrm((L, 2, C_AAA_LORA, C_W), 0.5 * C_AAA_LORA ** -0.5),
        'c_w_gate': nrm((L, C_GATE_LORA, C_W), C_GATE_LORA ** -0.5),
        'c_k_k': 0.85 + nrm((L, C_W), 0.05),
        'c_k_a': gain((L, C_W)),
        'c_r_k': nrm((L, C_HEADS, HEAD_DIM), 0.1),
        'c_gn_w': gain((L, C_W)),
        'c_gn_b': nrm((L, C_W), 0.02),
        'd_rel_bias': nrm((L, D_HEADS, 2 * NA_ROWS - 1, 2 * NA_COLS - 1), 0.2),
        'w_branch': nrm((L, N_BRANCH, BRANCH_W, D), BRANCH_W ** -0.5),
        'w_out': nrm((L, D, D), D ** -0.5),
        'w_mlp1': nrm((L, D, D_FF), D ** -0.5),
        'w_mlp2': nrm((L, D_FF, D), D_FF ** -0.5),
        'g_final': gain((D,)),
    }

def reference(x, c, ctx, c_ctx, w_ada, b_ada, g_norm1, g_norm2, w_in, a_q_gain, a_k_gain, b_q_gain, b_kv_gain,
              b_w_q_up, b_w_kv_up, c_mu, c_w0, c_w_decay, c_a0, c_w_aaa, c_w_gate, c_k_k, c_k_a, c_r_k,
              c_gn_w, c_gn_b, d_rel_bias, w_branch, w_out, w_mlp1, w_mlp2, g_final):
    s = x.shape[1]
    t = jnp.arange(s)
    rows = t // GRID_W
    cols = t % GRID_W
    xc = ctx
    for l in range(DEPTH):
        mod_lat = (jax.nn.silu(c) @ w_ada[l] + b_ada[l])[:, None, :]
        mod_ctx = (jax.nn.silu(c_ctx) @ w_ada[l] + b_ada[l])[None, None, :]
        lp = dict(g_norm1=g_norm1[l], g_norm2=g_norm2[l], w_in=w_in[l],
                  a_q_gain=a_q_gain[l], a_k_gain=a_k_gain[l],
                  b_q_gain=b_q_gain[l], b_kv_gain=b_kv_gain[l], b_w_q_up=b_w_q_up[l], b_w_kv_up=b_w_kv_up[l],
                  c_mu=c_mu[l], c_w0=c_w0[l], c_w_decay=c_w_decay[l], c_a0=c_a0[l], c_w_aaa=c_w_aaa[l],
                  c_w_gate=c_w_gate[l], c_k_k=c_k_k[l], c_k_a=c_k_a[l], c_r_k=c_r_k[l],
                  c_gn_w=c_gn_w[l], c_gn_b=c_gn_b[l], d_rel_bias=d_rel_bias[l],
                  w_branch=w_branch[l], w_out=w_out[l], w_mlp1=w_mlp1[l], w_mlp2=w_mlp2[l])
        x, xc = _layer(x, xc, rows, cols, mod_lat, mod_ctx, lp, l == DEPTH - 1)
    return rms_norm(x, g_final)


_drawn_inputs = setup_inputs


def setup_inputs(seed=0):
    import zlib

    import numpy as np

    out = dict(_drawn_inputs(seed))
    spreads = {}
    factors = {'g_norm1': 4.396,
     'a_q_gain': 8.0,
     'a_k_gain': 8.0,
     'b_q_gain': 8.0,
     'b_kv_gain': 8.0,
     'b_w_q_up': 2.718,
     'c_w_decay': 6.382,
     'c_w_aaa': 2.669,
     'c_k_k': 31.928,
     'c_k_a': 4.077,
     'c_gn_w': 29.522,
     'c_gn_b': 64.0,
     'd_rel_bias': 8.0,
     'g_norm2': 7.075}
    for name, (base, spread) in spreads.items():
        noise = np.random.default_rng([zlib.crc32(name.encode()), seed]).standard_normal(out[name].shape)
        drawn = base * np.exp(spread * noise) if base else spread * noise
        out[name] = __import__('jax').numpy.asarray(drawn.astype(out[name].dtype))
    for name, factor in factors.items():
        out[name] = (out[name] * factor).astype(out[name].dtype)
    return out
```

```python
import numpy as np
from contextlib import ExitStack

import concourse.bass as bass
from concourse import mybir

P = 128
D_MODEL, DEPTH = 1024, 2
CTX, SEQ = 256, 256
T = CTX + SEQ
KT = D_MODEL // P
D_FF = 4 * D_MODEL
HEADS, HD = 8, 64
PAIRS = HEADS // 2
B_QL, B_KVL, B_NOPE, B_ROPE = 384, 256, 64, 32
B_QD = B_NOPE + B_ROPE
GRID_W, NA_COLS, NA_ROWS = 64, 16, 8
A_Q, A_KV = 512, 128
C_W = 512
OFF_A = 0
OFF_B = OFF_A + A_Q + 2 * A_KV
OFF_C = OFF_B + B_QL + B_KVL + B_ROPE
OFF_D = OFF_C + 3 * C_W + 2 * 64 + 2 * 64 + 128
OFF_G = OFF_D + 3 * 512
NORM_EPS, GN_EPS = 1e-6, 64e-5
CHUNK = 64
NCH = T // CHUNK
DECAY = float(np.exp(-0.5))

PANEL = KT * P
N_ADA, N_C, N_A, N_B, N_D = 48, 15, 6, 6, 12
N_MERGE, N_OUT, N_UP, N_DOWN = 48, 8, 32, 32
N_PANELS = N_ADA + N_C + N_A + N_B + N_D + N_MERGE + N_OUT + N_UP + N_DOWN
SLOTS = 6

VEC = {}
_at = 0
for _name, _n in (("b_ada", 48), ("g1", 8), ("g2", 8), ("a_q", 1), ("a_k", 1), ("b_q", 3), ("b_kv", 2), ("mu", 15),
                  ("w0", 8), ("a0", 8), ("k_k", 4), ("k_a", 4), ("r_k", 4), ("gn_w", 4), ("gn_b", 4), ("g_final", 8)):
    VEC[_name] = _at
    _at += _n
N_VEC = _at

G_ID, G_ONE, G_BLK, G_EPS = 0, P, 2 * P, 3 * P
N_GC = 3 * P + 4
T_PA, T_PB, T_CA, T_SA, T_CB, T_SB = 0, P, 2 * P, 2 * P + SEQ, 2 * P + 2 * SEQ, 2 * P + 3 * SEQ
N_TC = 2 * P + 4 * SEQ
LEVELS = 6
R_STRICT, R_INCL, R_LEVEL = 0, P, 2 * P
R_DIR = 2 * P + LEVELS * P
R_RESET = 2 * R_DIR
N_RC = R_RESET + 2 * T
SB_Q, SB_K, SB_V = 0, 3 * 8 * B_QD, 3 * 8 * B_QD + 2 * 512
N_SB = SB_V + 2 * 512
SC_DEC, SC_AAA, SC_GATE = 0, 512, 1024
N_SC = 1536


def _panel(w):
    k, n = w.shape
    out = np.zeros((P, k // P, P), w.dtype)
    out[:, :, :n] = w.reshape(k // P, P, n).transpose(1, 0, 2)
    return out


def _lay_panels(w_ada, w_in, w_branch, w_out, w_mlp1, w_mlp2):
    out = np.zeros((DEPTH, N_PANELS, P, KT, P), w_in.dtype)
    for l in range(DEPTH):
        n = [0]

        def put(p):
            out[l, n[0], :, :p.shape[1]] = p
            n[0] += 1

        def cols(w, at, count):
            for j in range(count):
                put(_panel(w[:, at + j * P:at + (j + 1) * P]))

        wi = w_in[l]
        cols(w_ada[l], 0, N_ADA)
        cols(wi, OFF_C, N_C)
        for t in range(4):
            put(_panel(np.concatenate([wi[:, OFF_A + 64 * t:][:, :64], wi[:, OFF_A + 64 * (t + 4):][:, :64]], 1)))
        cols(wi, OFF_A + A_Q, 2)
        cols(wi, OFF_B, 5)
        put(_panel(np.concatenate([np.zeros((D_MODEL, 64), wi.dtype), wi[:, OFF_B + 640:OFF_B + 672]], 1)))
        cols(wi, OFF_D, N_D)
        wb = []
        for i in range(4):
            w = w_branch[l, i]
            if i == 0:
                w = w.reshape(2, 4, 64, D_MODEL).transpose(1, 0, 2, 3).reshape(512, D_MODEL)
            wb.append(w)
        for m in range(KT):
            for i in (0, 2):
                for g in (i, i + 1):
                    put(_panel(wi[:, OFF_G + g * D_MODEL + m * P:][:, :P]))
                put(np.concatenate([_panel(wb[g][:, m * P:(m + 1) * P]) for g in (i, i + 1)], 1))
        cols(w_out[l], 0, N_OUT)
        cols(w_mlp1[l], 0, N_UP)
        for m in range(KT):
            for q in range(4):
                put(_panel(w_mlp2[l, q * D_MODEL:(q + 1) * D_MODEL, m * P:(m + 1) * P]))
        assert n[0] == N_PANELS
    return out.reshape(DEPTH, N_PANELS, P, PANEL)


def _lay_vectors(v):
    out = np.zeros((DEPTH, P, N_VEC), np.float32)
    for l in range(DEPTH):
        def put(name, a, n):
            out[l, :, VEC[name]:VEC[name] + n] = a.reshape(n, P).T

        put("b_ada", v["b_ada"][l], 48)
        put("g1", v["g_norm1"][l], 8)
        put("g2", v["g_norm2"][l], 8)
        put("a_q", np.concatenate([v["a_q_gain"][l]] * 2), 1)
        put("a_k", np.concatenate([v["a_k_gain"][l]] * 2), 1)
        put("b_q", v["b_q_gain"][l], 3)
        put("b_kv", v["b_kv_gain"][l], 2)
        put("mu", v["c_mu"][l], 15)
        put("w0", v["c_w0"][l], 8)
        put("a0", v["c_a0"][l], 8)
        put("k_k", v["c_k_k"][l], 4)
        put("k_a", v["c_k_a"][l], 4)
        put("r_k", v["c_r_k"][l], 4)
        put("gn_w", v["c_gn_w"][l], 4)
        put("gn_b", v["c_gn_b"][l], 4)
        put("g_final", v["g_final"], 8)
    return out


def _lay_small(b_w_q_up, b_w_kv_up, c_w_decay, c_w_aaa, c_w_gate):
    sb = np.zeros((DEPTH, P, N_SB), np.float32)
    sc = np.zeros((DEPTH, P, N_SC), np.float32)
    for l in range(DEPTH):
        sb[l, :, SB_Q:SB_K] = b_w_q_up[l].reshape(3, P, 8 * B_QD).transpose(1, 0, 2).reshape(P, -1)
        kv = b_w_kv_up[l].reshape(2, P, 8, 2, 64)
        sb[l, :, SB_K:SB_V] = kv[:, :, :, 0].transpose(1, 0, 2, 3).reshape(P, -1)
        sb[l, :, SB_V:] = kv[:, :, :, 1].transpose(1, 0, 2, 3).reshape(P, -1)
        sc[l, :, SC_DEC:SC_AAA] = c_w_decay[l].reshape(P, 512)
        sc[l, :, SC_AAA:SC_GATE] = c_w_aaa[l].reshape(P, 512)
        sc[l, :, SC_GATE:] = c_w_gate[l]
    return sb, sc


def _lay_bias(rel_bias):
    out = np.full((DEPTH, HEADS, SEQ, SEQ), -1e30, np.float32)
    rows = SEQ // GRID_W
    for c in range(GRID_W):
        c0 = min(max(c - NA_COLS // 2, 0), GRID_W - NA_COLS)
        d0 = c0 - c + NA_COLS - 1
        for r in range(rows):
            for rk in range(rows):
                out[:, :, r * GRID_W + c, rk * GRID_W + c0:rk * GRID_W + c0 + NA_COLS] = \
                    rel_bias[:, :, rk - r + NA_ROWS - 1, d0:d0 + NA_COLS]
    return np.ascontiguousarray(out.reshape(DEPTH, HEADS, 2, P, SEQ).transpose(0, 2, 3, 1, 4))


def _shape_constants():
    g = np.zeros((P, N_GC), np.float32)
    g[:, G_ID:G_ID + P] = np.eye(P)
    g[:, G_ONE:G_ONE + P] = 1
    g[:64, G_BLK:G_BLK + 64] = 1
    g[64:, G_BLK + 64:G_BLK + P] = 1
    g[:, G_EPS] = NORM_EPS
    g[:, G_EPS + 1] = GN_EPS
    t = np.zeros((P, N_TC), np.float32)
    t[:, T_CA:T_CA + SEQ] = 1
    t[:, T_CB:T_CB + SEQ] = 1
    tok = np.arange(SEQ)
    pos = (tok // GRID_W, tok % GRID_W)

    def rotary(base, width, perm, cos, sin):
        half = width // 4
        inv = (np.float32(10000.0) ** (-np.arange(half, dtype=np.float32) / half)).astype(np.float32)
        for s in range(2):
            ang = pos[s].astype(np.float32)[:, None] * inv[None, :]
            for i in range(half):
                a, b = base + s * 2 * half + i, base + s * 2 * half + half + i
                t[a, cos:cos + SEQ] = t[b, cos:cos + SEQ] = np.cos(ang[:, i])
                t[a, sin:sin + SEQ] = t[b, sin:sin + SEQ] = np.sin(ang[:, i])
                t[b, perm + a] = -1
                t[a, perm + b] = 1

    rotary(0, 64, T_PA, T_CA, T_SA)
    rotary(64, 64, T_PA, T_CA, T_SA)
    rotary(64, 32, T_PB, T_CB, T_SB)
    r = np.zeros((P, N_RC), np.float32)
    i = np.arange(P)
    same = (i[:, None] // CHUNK) == (i[None, :] // CHUNK)
    for d in range(2):
        before = (i[:, None] < i[None, :]) if d == 0 else (i[:, None] > i[None, :])
        at = d * R_DIR
        r[:, at + R_STRICT:at + R_STRICT + P] = same & before
        r[:, at + R_INCL:at + R_INCL + P] = same & (before | np.eye(P, dtype=bool))
        for j in range(LEVELS):
            pair = ((i[:, None] >> (j + 1)) == (i[None, :] >> (j + 1))) & ((i[:, None] >> j) != (i[None, :] >> j))
            r[:, at + R_LEVEL + j * P:at + R_LEVEL + (j + 1) * P] = pair & before
        tokens = np.arange(T)
        first = tokens % CHUNK == (0 if d == 0 else CHUNK - 1)
        r[:, R_RESET + d * T:R_RESET + (d + 1) * T] = ~first
    return g, t, r


def build(nc, x_t, c_cols, panels, vectors, small_b, small_c, bias_d, const_g, const_t, const_r, out_t):
    f32, u32 = mybir.dt.float32, mybir.dt.uint32
    ALU, ACT, AX = mybir.AluOpType, mybir.ActivationFunctionType, mybir.AxisListType
    ctx = ExitStack()

    def sb(name, cols):
        return ctx.enter_context(nc.sbuf_tensor(name, [P, cols], f32))

    sems, totals = {}, {}

    class Sem:

        def __init__(self, name, base):
            if name not in sems:
                sems[name] = ctx.enter_context(nc.semaphore(name))
            self.h, self.base = sems[name], base

        def at(self, n):
            return self.base + n

    def sem(name, total=None):
        base = totals.get(name, 0)
        if total is not None:
            totals[name] = base + total
        return Sem(name, base if total is not None else 0)

    own = {}

    def link(e, instruction):
        step = own[id(e)]
        step[1] += 1
        instruction.then_inc(step[0], 1)
        e.wait_ge(step[0], step[1])

    class Banks:

        def __init__(self, name, banks, total=None, free=None):
            self.full, self.free, self.banks = sem(name + "_full", total), free or sem(name + "_free", total), banks
            self.filled = self.emptied = 0

        def take(self):
            self.filled += 1
            bank = psum[:, self.banks[(self.filled - 1) % len(self.banks)], :]
            return bank, self.filled - len(self.banks)

        def arrived(self):
            self.emptied += 1
            return psum[:, self.banks[(self.emptied - 1) % len(self.banks)], :], self.emptied

    psum = ctx.enter_context(nc.psum_tensor("psum", [P, 8, 512], f32))
    x = sb("x_stream", KT * T)[:, :].rearrange("p (k t) -> p k t", k=KT)
    h = sb("normed", KT * T)[:, :].rearrange("p (k t) -> p k t", k=KT)
    ring = sb("panel_ring", SLOTS * PANEL)[:, :].rearrange("p (s k m) -> p s k m", s=SLOTS, k=KT)
    gc = sb("const_global", N_GC)
    vec = sb("vectors_sb", DEPTH * N_VEC)[:, :].rearrange("p (l n) -> p l n", l=DEPTH)
    csil = sb("c_silu", 3 * KT * 2)[:, :].rearrange("p (a n) -> p a n", a=3)
    mod = sb("modulation", 48 * 2)[:, :].rearrange("p (j s) -> p j s", s=2)
    sc_h = sb("norm_scales", 2 * KT * 2)[:, :].rearrange("p (a k s) -> p a k s", a=2, k=KT)
    drv = sb("derived_vectors", 64)
    stat = sb("softmax_stats", 3 * 8)[:, :].rearrange("p (a n) -> p a n", a=3)
    ARENA = 35600
    arena = sb("arena", ARENA)
    ident, ones, blk = gc[:, G_ID:G_ID + P], gc[:, G_ONE:G_ONE + P], gc[:, G_BLK:G_BLK + P]
    eps, gn_eps = gc[:, G_EPS:G_EPS + 1], gc[:, G_EPS + 1:G_EPS + 2]

    def carve(at, *shape):
        n = 1
        for s in shape:
            n *= s
        assert at + n <= ARENA
        ap = arena[:, at:at + n]
        if len(shape) == 2:
            ap = ap.rearrange("p (a b) -> p a b", a=shape[0])
        elif len(shape) == 3:
            ap = ap.rearrange("p (a b c) -> p a b c", a=shape[0], b=shape[1])
        elif len(shape) == 4:
            ap = ap.rearrange("p (a b c d) -> p a b c d", a=shape[0], b=shape[1], c=shape[2])
        return ap

    def carver(at=0):
        pos = [at]

        def take(*shape):
            ap = carve(pos[0], *shape)
            n = 1
            for s in shape:
                n *= s
            pos[0] += n
            return ap
        return take, pos

    o_c = sb("out_c", 4 * T)[:, :].rearrange("p (k t) -> p k t", k=4)
    END = ARENA - 3 * 4 * T
    o_a, o_b, o_d = (carve(END + i * 4 * T, 4, T) for i in range(3))
    branch = [o_a, o_b, o_c, o_d]

    stages = []
    mid, full_row = slice(CTX, T), slice(0, T)

    class Panels:

        def __init__(self):
            self.n = 0

        def take(self):
            slot = self.n % SLOTS
            self.n += 1
            return ring[:, slot, :, :], panel_in[slot], 16 * ((self.n - 1) // SLOTS + 1)

    panel_in = [sem(f"panel_in_{s}") for s in range(SLOTS)]
    panels_begun = sem("panels_begun")
    stream = Panels()

    def mm(out, lhsT, rhs, start, stop, check=False):
        return nc.tensor.matmul(out, lhsT, rhs, start=start, stop=stop, skip_group_check=check)

    def panel_fm(e, banks, src, tok):
        ps, n_free = banks.take()
        if n_free > 0:
            e.wait_ge(banks.free.h, banks.free.at(n_free))
        w, slot_in, n_in = stream.take()
        e.wait_ge(slot_in.h, n_in)
        for k in range(KT):
            i = mm(ps[:, :tok.stop - tok.start], w[:, k, :], src[:, k, tok], k == 0, k == KT - 1)
            if k == 0:
                i.then_inc(panels_begun.h, 1)
        i.then_inc(banks.full.h, 1)

    def panel_tm(e, ps, full):
        w, slot_in, n_in = stream.take()
        e.wait_ge(slot_in.h, n_in)
        for tt in range(4):
            for k in range(KT):
                i = mm(ps[:, tt * P:(tt + 1) * P], h[:, k, tt * P:(tt + 1) * P], w[:, k, :], k == 0, k == KT - 1)
                if tt == 0 and k == 0:
                    i.then_inc(panels_begun.h, 1)
        i.then_inc(full.h, 1)

    def stage_ada(l):
        b = Banks("ada", [0], 1)
        silu_done, c_tanh = sem("silu_done"), sem("c_tanh")
        row_full, row_ready = sem("ada_row_full", 12), sem("ada_row_ready", 12)
        rows = carve(0, 48 * P)

        def act(e):
            if l == 0:
                e.wait_ge(sem("small_in").h, sem("small_in").at(16 * 4))
                nc.scalar.activation(csil[:, 1, :], csil[:, 0, :], ACT.Tanh, scale=0.5).then_inc(c_tanh.h, 1)
            for g in range(12):
                e.wait_ge(row_full.h, row_full.at(g + 1))
                nc.scalar.activation(rows[:2, g * 512:(g + 1) * 512], psum[:2, 1 + g % 4, :], ACT.Copy).then_inc(row_ready.h, 1)

        def dve(e):
            if l == 0:
                e.wait_ge(sem("small_in").h, sem("small_in").at(16 * 4))
                e.wait_ge(c_tanh.h, c_tanh.at(1))
                link(e, nc.vector.tensor_scalar(csil[:, 1, :], csil[:, 1, :], 1.0, 0.5, ALU.add, ALU.mult))
                nc.vector.tensor_tensor(csil[:, 2, :], csil[:, 1, :], csil[:, 0, :], ALU.mult).then_inc(silu_done.h, 1)
            ps, n_full = b.arrived()
            e.wait_ge(b.full.h, b.full.at(n_full))
            bada = vec[:, l, VEC["b_ada"]:VEC["b_ada"] + 48].unsqueeze(2).broadcast_to([P, 48, 2])
            nc.vector.tensor_tensor(mod[:, :, :], ps[:, :96].rearrange("p (j s) -> p j s", s=2), bada, ALU.add).then_inc(b.free.h, 1)
            e.wait_ge(b.free.h, b.free.at(1))
            for a, g in ((0, "g1"), (1, "g2")):
                j = 8 + 24 * a
                gain = vec[:, l, VEC[g]:VEC[g] + KT].unsqueeze(2).broadcast_to([P, KT, 2])
                nc.vector.scalar_tensor_tensor(sc_h[:, a, :, :], mod[:, j:j + 8, :], 1.0, gain, ALU.add, ALU.mult)
            for dst, name, n, m, o in ((0, "w0", 8, 0.5, 0.0), (8, "a0", 8, 0.5, 0.0), (16, "k_a", 4, 0.5, 0.0),
                                       (20, "k_a", 4, -0.5, 1.0), (24, "mu", 15, -1.0, 1.0), (39, "mu", 15, 0.5, 0.0),
                                       (54, "a_q", 1, HD ** -0.5, 0.0)):
                nc.vector.tensor_scalar(drv[:, dst:dst + n], vec[:, l, VEC[name]:VEC[name] + n], m, o,
                                             ALU.mult, ALU.add)

        def pe(e):
            if l == 0:
                e.wait_ge(silu_done.h, silu_done.at(1))
            sil = csil[:, 2, :].rearrange("p (k s) -> p k s", s=2)
            for g in range(12):
                if g >= 4:
                    e.wait_ge(row_ready.h, row_ready.at(g - 3))
                for j in range(4):
                    w, slot_in, n_in = stream.take()
                    e.wait_ge(slot_in.h, n_in)
                    for k in range(KT):
                        p = mm(psum[:2, 1 + g % 4, j * P:(j + 1) * P], sil[:, k, :], w[:, k, :], k == 0, k == KT - 1)
                        if k == 0:
                            p.then_inc(panels_begun.h, 1)
                p.then_inc(row_full.h, 1)
            for g in range(12):
                e.wait_ge(row_ready.h, row_ready.at(g + 1))
                for j in range(4 * g, 4 * g + 4):
                    p = nc.tensor.transpose(psum[:, 0, 2 * j:2 * j + 2], rows[:2, j * P:(j + 1) * P], ident[:2, :2])
            p.then_inc(b.full.h, 1)

        def pool(e):
            if l == 0:
                for dst, src in ((gc[:, :], const_g), (csil[:, 0, :], c_cols),
                                 (vec[:, :, :], vectors.rearrange("l p n -> p l n")),
                                 (x, x_t.rearrange("(k p) t -> p k t", p=P))):
                    e.dma_start(dst, src).then_inc(sem("small_in").h, 16)
        stages.append((f"ada{l}", dict(pe=pe, act=act, dve=dve, pool=pool)))

    def stage_norm(name, l, which, tok, final=False):
        b = Banks("norm", [0], 1)
        squared, scaled = sem("norm_squared", KT), sem("norm_scaled", KT)
        n = tok.stop - tok.start
        rstd = carve(0, T)

        def act(e):
            e.wait_ge(sem("small_in").h, sem("small_in").at(16 * 4))
            for k in range(KT):
                nc.scalar.activation(h[:, k, tok], x[:, k, tok], ACT.Square).then_inc(squared.h, 1)
            ps, n_full = b.arrived()
            e.wait_ge(b.full.h, b.full.at(n_full))
            nc.scalar.activation(rstd[:, :n], ps[:, :n], ACT.Sqrt, bias=eps, scale=1.0 / D_MODEL).then_inc(b.free.h, 1)
            if final:
                return
            for k in range(KT):
                e.wait_ge(scaled.h, scaled.at(k + 1))
                for s, seg in ((0, slice(0, CTX)), (1, mid)):
                    if seg.start >= tok.start:
                        shift = mod[:, (0 if which == 0 else 24) + k, s:s + 1]
                        nc.scalar.activation(h[:, k, seg], h[:, k, seg], ACT.Identity, bias=shift,
                                                  scale=sc_h[:, which, k, s:s + 1])

        def dve(e):
            e.wait_ge(b.free.h, b.free.at(1))
            link(e, nc.vector.reciprocal(rstd[:, :n], rstd[:, :n]))
            for k in range(KT):
                if final:
                    g = vec[:, l, VEC["g_final"] + k:VEC["g_final"] + k + 1]
                    nc.vector.scalar_tensor_tensor(h[:, k, tok], x[:, k, tok], g, rstd[:, :n], ALU.mult, ALU.mult).then_inc(scaled.h, 1)
                else:
                    nc.vector.tensor_tensor(h[:, k, tok], x[:, k, tok], rstd[:, :n], ALU.mult).then_inc(scaled.h, 1)

        def pe(e):
            ps, n_free = b.take()
            if n_free > 0:
                e.wait_ge(b.free.h, b.free.at(n_free))
            for k in range(KT):
                e.wait_ge(squared.h, squared.at(k + 1))
                p = mm(ps[:, :n], ones, h[:, k, tok], k == 0, k == KT - 1)
                if k == KT - 1:
                    p.then_inc(b.full.h, 1)
        stages.append((name, dict(pe=pe, act=act, dve=dve)))

    def stage_attention(kind, l, q_of, k_of, v_of, out, tiles, bias, at):
        nm = f"{kind}{l}"
        take, _ = carver(at)
        prob, probT = take(3, T), take(3, 4, P)
        items = [(t, qt, nk, i) for t in range(PAIRS) for qt, nk in tiles for i in range(2)]
        n_items = len(items)
        scores_full, probsT_full, negmax_ready, exp_done, probs_ready, probsT_ready, pv_done = (
            sem("attention_" + n, n_items)
            for n in ("scores_full", "probsT_full", "negmax", "exp_done", "probs_ready", "probsT_ready", "pv_done"))
        out_free = sem("attention_out_free", n_items // 2)

        def pe(e):
            for s in range(n_items + 3):
                if s < n_items:
                    t, qt, nk, i = items[s]
                    if s - 2 > 0:
                        e.wait_ge(exp_done.h, exp_done.at(s - 2))
                    ps = psum[:, s % 3, :]
                    mm(ps[:, :nk], q_of(t, i, qt), k_of(t, i, nk), True, True).then_inc(scores_full.h, 1)
                if s >= 2 and s - 2 < n_items:
                    n = s - 2
                    nk = items[n][2]
                    e.wait_ge(probs_ready.h, probs_ready.at(n + 1))
                    if n - 2 > 0:
                        e.wait_ge(probsT_ready.h, probsT_ready.at(n - 2))
                    ps = psum[:, 3 + n % 3, :]
                    for kt in range(nk // P):
                        i_ = nc.tensor.transpose(ps[:, kt * P:(kt + 1) * P], prob[:, n % 3, kt * P:(kt + 1) * P], ident)
                        if kt == nk // P - 1:
                            i_.then_inc(probsT_full.h, 1)
                if s >= 3:
                    n = s - 3
                    t, qt, nk, i = items[n]
                    e.wait_ge(probsT_ready.h, probsT_ready.at(n + 1))
                    if n // 2 - 1 > 0:
                        e.wait_ge(out_free.h, out_free.at(n // 2 - 1))
                    ps = psum[:, 6 + (n // 2) % 2, :]
                    for kt in range(nk // P):
                        p = mm(ps[i * 64:(i + 1) * 64, :P], v_of(t, i, kt), probT[:, n % 3, kt, :], kt == 0, kt == nk // P - 1)
                        if kt == nk // P - 1:
                            p.then_inc(pv_done.h, 1)

        def dve(e):
            for s in range(n_items + 3):
                if s < n_items:
                    t, qt, nk, i = items[s]
                    e.wait_ge(scores_full.h, scores_full.at(s + 1))
                    ps = psum[:, s % 3, :]
                    if bias is not None and nk == T:
                        link(e, nc.vector.tensor_tensor(ps[:, mid], ps[:, mid], bias(t, i, qt), ALU.add))
                    nc.vector.tensor_reduce(stat[:, 0, s % 8:s % 8 + 1], ps[:, :nk], AX.X, ALU.max, negate=True).then_inc(negmax_ready.h, 1)
                if s >= 1 and s - 1 < n_items:
                    n = s - 1
                    nk = items[n][2]
                    e.wait_ge(exp_done.h, exp_done.at(n + 1))
                    link(e, nc.vector.reciprocal(stat[:, 2, n % 8:n % 8 + 1], stat[:, 1, n % 8:n % 8 + 1]))
                    nc.vector.tensor_scalar(prob[:, n % 3, :nk], prob[:, n % 3, :nk], stat[:, 2, n % 8:n % 8 + 1],
                                                 None, ALU.mult).then_inc(probs_ready.h, 1)
                if s >= 3 and (s - 3) % 2 == 1:
                    n = s - 3
                    t, qt, nk, i = items[n]
                    e.wait_ge(pv_done.h, pv_done.at(n + 1))
                    nc.vector.tensor_copy(out[:, t, qt * P:(qt + 1) * P], psum[:, 6 + (n // 2) % 2, :P]).then_inc(out_free.h, 1)

        def act(e):
            for s in range(n_items + 2):
                if s < n_items:
                    nk = items[s][2]
                    e.wait_ge(negmax_ready.h, negmax_ready.at(s + 1))
                    nc.scalar.activation(prob[:, s % 3, :nk], psum[:, s % 3, :nk], ACT.Exp,
                                              bias=stat[:, 0, s % 8:s % 8 + 1], accum_out=stat[:, 1, s % 8:s % 8 + 1]).then_inc(exp_done.h, 1)
                if s >= 2:
                    n = s - 2
                    nk = items[n][2]
                    e.wait_ge(probsT_full.h, probsT_full.at(n + 1))
                    if n - 2 > 0:
                        e.wait_ge(pv_done.h, pv_done.at(n - 2))
                    nc.scalar.activation(probT[:, n % 3, :nk // P, :].rearrange("p a b -> p (a b)"),
                                              psum[:, 3 + n % 3, :nk], ACT.Copy).then_inc(probsT_ready.h, 1)
        stages.append((nm + "_attention", dict(pe=pe, act=act, dve=dve)))

    def query_tiles(l):
        return [(qt, CTX) for qt in range(2) if l < DEPTH - 1] + [(qt, T) for qt in (2, 3)]

    def stage_a(l):
        nm = f"A{l}"
        take, pos = carver()
        consts, qk, v = take(N_TC), take(5, T), take(4, P)
        sq, tmp = take(2, T), take(2, T)
        att = pos[0]
        proj, sums, rots = Banks("a_proj", [0, 1, 2], 5), Banks("a_sums", [3, 4], 5), Banks("a_rot", [5, 6], 5)
        squared, normed, vfull = sem("a_squared", 5), sem("a_normed", 5), sem("a_v_full", 1)

        def pool(e):
            e.dma_start(consts, const_t).then_inc(sem(nm + "_consts_in").h, 16)

        def pe(e):
            for s in range(5 + 2):
                if s < 5:
                    panel_fm(e, proj, h, full_row)
                if s == 5:
                    panel_tm(e, psum[:, 7, :], vfull)
                if 1 <= s <= 5:
                    e.wait_ge(squared.h, squared.at(s))
                    ps, n_free = sums.take()
                    if n_free > 0:
                        e.wait_ge(sums.free.h, sums.free.at(n_free))
                    mm(ps, blk, sq[:, (s - 1) % 2, :], True, True).then_inc(sums.full.h, 1)
                if s >= 2:
                    if s == 2:
                        e.wait_ge(sem(nm + "_consts_in").h, sem(nm + "_consts_in").at(16))
                    if s - 1 > 0:
                        e.wait_ge(normed.h, normed.at(s - 1))
                    ps, n_free = rots.take()
                    if n_free > 0:
                        e.wait_ge(rots.free.h, rots.free.at(n_free))
                    mm(ps[:, :SEQ], consts[:, T_PA:T_PA + P], qk[:, s - 2, mid], True, True).then_inc(rots.full.h, 1)

        def act(e):
            for j in range(6):
                if j < 5:
                    if j - 1 > 0:
                        e.wait_ge(sums.full.h, sums.full.at(j - 1))
                    e.wait_ge(proj.full.h, proj.full.at(j + 1))
                    ps = psum[:, j % 3, :]
                    nc.scalar.activation(sq[:, j % 2, :], ps, ACT.Square).then_inc(squared.h, 1)
                    nc.scalar.activation(qk[:, j, :], ps, ACT.Copy).then_inc(proj.free.h, 1)
                if j >= 1:
                    ps, n_full = sums.arrived()
                    e.wait_ge(sums.full.h, sums.full.at(n_full))
                    if j - 2 > 0:
                        e.wait_ge(normed.h, normed.at(j - 2))
                    nc.scalar.activation(tmp[:, (j - 1) % 2, :], ps, ACT.Sqrt, bias=eps, scale=1.0 / HD).then_inc(sums.free.h, 1)
            e.wait_ge(vfull.h, vfull.at(1))
            nc.scalar.activation(v.rearrange("p a b -> p (a b)"), psum[:, 7, :], ACT.Copy)

        def dve(e):
            for j in range(6):
                if j < 5:
                    e.wait_ge(sums.free.h, sums.free.at(j + 1))
                    r = tmp[:, j % 2, :]
                    link(e, nc.vector.reciprocal(r, r))
                    gain = drv[:, 54:55] if j < 4 else vec[:, l, VEC["a_k"]:VEC["a_k"] + 1]
                    nc.vector.scalar_tensor_tensor(qk[:, j, :], qk[:, j, :], gain, r, ALU.mult, ALU.mult).then_inc(normed.h, 1)
                if j >= 1:
                    k = j - 1
                    if k == 0:
                        e.wait_ge(sem(nm + "_consts_in").h, sem(nm + "_consts_in").at(16))
                    ps, n_full = rots.arrived()
                    e.wait_ge(rots.full.h, rots.full.at(n_full))
                    rot = sq3[:, k % 2, :]
                    nc.vector.tensor_tensor(rot, ps[:, :SEQ], consts[:, T_SA:T_SA + SEQ], ALU.mult).then_inc(rots.free.h, 1)
                    link(e, nc.vector.tensor_tensor(qk[:, k, mid], qk[:, k, mid], consts[:, T_CA:T_CA + SEQ], ALU.mult))
                    nc.vector.tensor_tensor(qk[:, k, mid], qk[:, k, mid], rot, ALU.add)
        sq3 = carve(att, 2, SEQ)
        stages.append((nm, dict(pe=pe, act=act, dve=dve, pool=pool)))
        assert att + 6 * T <= END
        stage_attention("A", l, lambda t, i, qt: qk[64 * i:64 * i + 64, t, qt * P:(qt + 1) * P],
                        lambda t, i, nk: qk[64 * i:64 * i + 64, 4, :nk], lambda t, i, kt: v[:, kt, 64 * i:64 * i + 64],
                        o_a, query_tiles(l), None, att)

    def stage_b(l):
        nm = f"B{l}"
        take, pos = carver()
        consts, small = take(N_TC), take(N_SB)
        lora, kr = take(5, T), take(T)
        q, k, v = take(8, T), take(8, T), take(4, 512)
        att = pos[0]
        sq, rs, rot = carve(att, 5, T), carve(att + 5 * T, 2, T), carve(att + 7 * T, 2, SEQ)
        assert att + 8 * T <= END
        w_q = small[:, SB_Q:SB_K].rearrange("p (k n) -> p k n", k=3)
        w_k = small[:, SB_K:SB_V].rearrange("p (k n) -> p k n", k=2)
        w_v = small[:, SB_V:].rearrange("p (k n) -> p k n", k=2)
        proj, sums = Banks("b_proj", [0, 1, 2], 5), Banks("b_sums", [3, 4], 2)
        up_ready = sem("b_up_ready", 20)
        up, rots, krb = Banks("b_up", [0, 1, 2], 20, free=up_ready), Banks("b_rot", [5, 6], 9), Banks("b_kr", [7], 1)
        squared, normed, kr_ready = sem("b_squared", 5), sem("b_normed", 5), sem("b_rotated", 9)
        groups = ((0, 3, B_QL, "b_q"), (3, 2, B_KVL, "b_kv"))
        kr_raw = sem("b_kr_raw", 1)

        def pool(e):
            e.dma_start(consts, const_t).then_inc(sem(nm + "_consts_in").h, 16)
            e.dma_start(small, small_b[l]).then_inc(sem(nm + "_consts_in").h, 16)
            e.wait_ge(kr_ready.h, kr_ready.at(1))
            for hd in range(8):
                nc.gpsimd.tensor_copy(k[64:96, hd, :], kr[64:96, :])

        def pe(e):
            for j in range(5):
                panel_fm(e, proj, h, full_row)
            panel_fm(e, krb, h, full_row)
            for j0, n, _, _ in groups:
                ps, n_free = sums.take()
                if n_free > 0:
                    e.wait_ge(sums.free.h, sums.free.at(n_free))
                for j in range(n):
                    e.wait_ge(squared.h, squared.at(j0 + j + 1))
                    p = mm(ps, ones, sq[:, j0 + j, :], j == 0, j == n - 1)
                    if j == n - 1:
                        p.then_inc(sums.full.h, 1)
            e.wait_ge(sem(nm + "_consts_in").h, sem(nm + "_consts_in").at(32))
            e.wait_ge(kr_raw.h, kr_raw.at(1))
            ps, n_free = rots.take()
            if n_free > 0:
                e.wait_ge(rots.free.h, rots.free.at(n_free))
            mm(ps[:P, :SEQ], consts[64:96, T_PB:T_PB + P], kr[64:96, mid], True, True).then_inc(rots.full.h, 1)
            e.wait_ge(proj.free.h, proj.free.at(5))
            for hd in range(8):
                e.wait_ge(normed.h, normed.at(3))
                ps, n_free = up.take()
                if n_free > 0:
                    e.wait_ge(up.free.h, up.free.at(n_free))
                for kk in range(3):
                    p = mm(ps[:B_QD, :], w_q[:, kk, hd * B_QD:(hd + 1) * B_QD], lora[:, kk, :], kk == 0, kk == 2)
                    if kk == 2:
                        p.then_inc(up.full.h, 1)
                if hd >= 1:
                    e.wait_ge(up_ready.h, up_ready.at(hd))
                    ps, n_free = rots.take()
                    if n_free > 0:
                        e.wait_ge(rots.free.h, rots.free.at(n_free))
                    mm(ps[:P, :SEQ], consts[64:96, T_PB:T_PB + P], q[64:96, hd - 1, mid], True, True).then_inc(rots.full.h, 1)
            e.wait_ge(up_ready.h, up_ready.at(8))
            ps, n_free = rots.take()
            if n_free > 0:
                e.wait_ge(rots.free.h, rots.free.at(n_free))
            mm(ps[:P, :SEQ], consts[64:96, T_PB:T_PB + P], q[64:96, 7, mid], True, True).then_inc(rots.full.h, 1)
            e.wait_ge(normed.h, normed.at(5))
            for hd in range(8):
                ps, n_free = up.take()
                if n_free > 0:
                    e.wait_ge(up.free.h, up.free.at(n_free))
                for kk in range(2):
                    p = mm(ps[:64, :], w_k[:, kk, hd * 64:(hd + 1) * 64], lora[:, 3 + kk, :], kk == 0, kk == 1)
                    if kk == 1:
                        p.then_inc(up.full.h, 1)
            for tt in range(4):
                ps, n_free = up.take()
                if n_free > 0:
                    e.wait_ge(up.free.h, up.free.at(n_free))
                for kk in range(2):
                    p = mm(ps, lora[:, 3 + kk, tt * P:(tt + 1) * P], w_v[:, kk, :], kk == 0, kk == 1)
                    if kk == 1:
                        p.then_inc(up.full.h, 1)

        def act(e):
            for j in range(5):
                ps, n_full = proj.arrived()
                e.wait_ge(proj.full.h, proj.full.at(n_full))
                nc.scalar.activation(sq[:, j, :], ps, ACT.Square).then_inc(squared.h, 1)
                nc.scalar.activation(lora[:, j, :], ps, ACT.Copy).then_inc(proj.free.h, 1)
            ps, n_full = krb.arrived()
            e.wait_ge(krb.full.h, krb.full.at(n_full))
            nc.scalar.activation(kr[64:96, :], ps[64:96, :], ACT.Copy).then_inc(kr_raw.h, 1)
            for g, (_, _, width, _) in enumerate(groups):
                ps, n_full = sums.arrived()
                e.wait_ge(sums.full.h, sums.full.at(n_full))
                nc.scalar.activation(rs[:, g, :], ps, ACT.Sqrt, bias=eps, scale=1.0 / width).then_inc(sums.free.h, 1)
            for hd in range(8):
                ps, n_full = up.arrived()
                e.wait_ge(up.full.h, up.full.at(n_full))
                nc.scalar.activation(q[:B_QD, hd, :], ps[:B_QD, :], ACT.Copy, scale=B_QD ** -0.5).then_inc(up_ready.h, 1)
            for hd in range(8):
                ps, n_full = up.arrived()
                e.wait_ge(up.full.h, up.full.at(n_full))
                nc.scalar.activation(k[:64, hd, :], ps[:64, :], ACT.Copy).then_inc(up_ready.h, 1)
            for tt in range(4):
                ps, n_full = up.arrived()
                e.wait_ge(up.full.h, up.full.at(n_full))
                nc.scalar.activation(v[:, tt, :], ps, ACT.Copy).then_inc(up_ready.h, 1)

        def rotate(e, dst, lo, hi):
            ps, n_full = rots.arrived()
            e.wait_ge(rots.full.h, rots.full.at(n_full))
            r = rot[lo:hi, rots.emptied % 2, :]
            nc.vector.tensor_tensor(r, ps[lo:hi, :SEQ], consts[lo:hi, T_SB:T_SB + SEQ], ALU.mult).then_inc(rots.free.h, 1)
            link(e, nc.vector.tensor_tensor(dst, dst, consts[lo:hi, T_CB:T_CB + SEQ], ALU.mult))
            nc.vector.tensor_tensor(dst, dst, r, ALU.add).then_inc(kr_ready.h, 1)

        def dve(e):
            for g, (j0, n, _, gain) in enumerate(groups):
                e.wait_ge(sums.free.h, sums.free.at(g + 1))
                link(e, nc.vector.reciprocal(rs[:, g, :], rs[:, g, :]))
                for j in range(n):
                    c = VEC[gain] + j
                    nc.vector.scalar_tensor_tensor(lora[:, j0 + j, :], lora[:, j0 + j, :], vec[:, l, c:c + 1],
                                                        rs[:, g, :], ALU.mult, ALU.mult).then_inc(normed.h, 1)
            e.wait_ge(sem(nm + "_consts_in").h, sem(nm + "_consts_in").at(32))
            rotate(e, kr[64:96, mid], 64, 96)
            for hd in range(8):
                e.wait_ge(up_ready.h, up_ready.at(hd + 1))
                rotate(e, q[64:96, hd, mid], 64, 96)
        stages.append((nm, dict(pe=pe, act=act, dve=dve, pool=pool)))
        stage_attention("B", l, lambda t, i, qt: q[:B_QD, 2 * t + i, qt * P:(qt + 1) * P],
                        lambda t, i, nk: k[:B_QD, 2 * t + i, :nk],
                        lambda t, i, kt: v[:, kt, (2 * t + i) * 64:(2 * t + i + 1) * 64], o_b, query_tiles(l), None, att)

    def stage_d(l):
        nm = f"D{l}"
        take, pos = carver()
        q, k, v, bias = take(4, T), take(4, T), take(4, 4, P), take(2, 8, SEQ)
        att = pos[0]
        assert att + 6 * T <= END
        proj = Banks("d_proj", [0, 1, 2], 12)

        def pool(e):
            e.dma_start(bias, bias_d[l].rearrange("a p h k -> p a h k")).then_inc(sem(nm + "_bias_in").h, 16)

        def pe(e):
            for j in range(8):
                panel_fm(e, proj, h, full_row)
            for j in range(4):
                ps, n_free = proj.take()
                e.wait_ge(proj.free.h, proj.free.at(n_free))
                panel_tm(e, ps, proj.full)

        def act(e):
            for j in range(12):
                ps, n_full = proj.arrived()
                e.wait_ge(proj.full.h, proj.full.at(n_full))
                dst = q[:, j, :] if j < 4 else k[:, j - 4, :] if j < 8 else v[:, :, j - 8, :]
                src = ps if j < 8 else ps.rearrange("p (a b) -> p a b", a=4)
                nc.scalar.activation(dst, src, ACT.Copy, scale=HD ** -0.5 if j < 4 else 1.0).then_inc(proj.free.h, 1)

        def dve(e):
            e.wait_ge(sem(nm + "_bias_in").h, sem(nm + "_bias_in").at(16))
        stages.append((nm, dict(pe=pe, act=act, dve=dve, pool=pool)))
        stage_attention("D", l, lambda t, i, qt: q[64 * i:64 * i + 64, t, qt * P:(qt + 1) * P],
                        lambda t, i, nk: k[64 * i:64 * i + 64, t, :nk],
                        lambda t, i, kt: v[:, kt, t, 64 * i:64 * i + 64], o_d, query_tiles(l),
                        lambda t, i, qt: bias[:, qt - 2, 2 * t + i, :], att)

    def stage_c(l):
        nm = f"C{l}"
        take, pos = carver()
        consts, small, z = take(N_RC), take(N_SC), take(15, T)
        base = pos[0]
        pad, nbr, own = take(3, 2, CTX + 2), take(3, 2, CTX), take(2, T)
        proj = Banks("c_proj", [0, 1, 2, 3], 15)
        summed, mixed, kept = sem("c_summed", 15), sem("c_mixed", 15), sem("c_kept", 15)
        zeroed, squashed = sem("c_zeroed", 1), sem("c_squashed", 2)

        def pool(e):
            e.dma_start(small, small_c[l]).then_inc(sem(nm + "_consts_in").h, 16)
            e.dma_start(consts, const_r).then_inc(sem(nm + "_consts_in").h, 16)
            nc.gpsimd.memset(pad.rearrange("p a s t -> p (a s t)"), 0.0).then_inc(zeroed.h, 1)
            for j in range(15):
                e.wait_ge(proj.free.h, proj.free.at(j + 1))
                if j - 2 > 0:
                    e.wait_ge(mixed.h, mixed.at(j - 2))
                nc.gpsimd.tensor_tensor(nbr[:, j % 3, :, :], pad[:, j % 3, :, 0:CTX], pad[:, j % 3, :, 2:CTX + 2],
                                             ALU.add).then_inc(summed.h, 1)

        def pe(e):
            for j in range(15):
                panel_fm(e, proj, h, full_row)

        def act(e):
            e.wait_ge(zeroed.h, zeroed.at(1))
            for j in range(15):
                ps, n_full = proj.arrived()
                e.wait_ge(proj.full.h, proj.full.at(n_full))
                if j - 2 > 0:
                    e.wait_ge(summed.h, summed.at(j - 2))
                if j - 2 > 0:
                    e.wait_ge(kept.h, kept.at(j - 2))
                nc.scalar.activation(pad[:, j % 3, :, 1:CTX + 1], ps.rearrange("p (s t) -> p s t", s=2), ACT.Copy).then_inc(proj.free.h, 1)
            for j, fn, scale in ((12, ACT.Tanh, 1.0), (14, ACT.Tanh, 0.5)):
                e.wait_ge(mixed.h, mixed.at(j + 1))
                nc.scalar.activation(z[:, j, :], z[:, j, :], fn, scale=scale).then_inc(squashed.h, 1)

        def dve(e):
            for j in range(15):
                e.wait_ge(proj.free.h, proj.free.at(j + 1))
                o = own[:, j % 2, :].rearrange("p (s t) -> p s t", s=2)
                nc.vector.tensor_scalar(o, pad[:, j % 3, :, 1:CTX + 1], drv[:, 24 + j:25 + j], None, ALU.mult).then_inc(kept.h, 1)
                e.wait_ge(summed.h, summed.at(j + 1))
                e.wait_ge(kept.h, kept.at(j + 1))
                nc.vector.scalar_tensor_tensor(z[:, j, :].rearrange("p (s t) -> p s t", s=2), nbr[:, j % 3, :, :],
                                                    drv[:, 39 + j:40 + j], o, ALU.mult, ALU.add).then_inc(mixed.h, 1)
            e.wait_ge(squashed.h, squashed.at(2))
            nc.vector.tensor_scalar(z[:, 14, :], z[:, 14, :], 1.0, 0.5, ALU.add, ALU.mult)
            e.wait_ge(sem(nm + "_consts_in").h, sem(nm + "_consts_in").at(32))
        stages.append((nm, dict(pe=pe, act=act, dve=dve, pool=pool)))
        for ft in range(4):
            stage_c_pair(l, ft, base, consts, small, z)

    def stage_c_pair(l, ft, base, consts, small, z):
        nm = f"Cp{l}{ft}"
        take, pos = carver(base)
        kk, kssum, vtm = take(T), take(T), take(4, P)
        lw, L, t2, e1, e2, e3 = take(T), take(T), take(T), take(T), take(T), take(T)
        al, be, ka, rh = take(T), take(T), take(T), take(T)
        cols = take(64)
        av = take(4, 2, 2, 64)
        btm, ktm = take(4, P), take(4, P)
        rmat = take(T)
        gt, hm, sm = take(NCH, P), take(NCH, P), take(NCH, P)
        per_head = [dict((n, take(4, P)) for n in ("N", "N_t", "M1", "M3", "M4", "X", "X_t", "B")) for _ in range(2)]
        wu = [take(4, P) for _ in range(2)]
        r, k, v = z[:, ft, :], z[:, 4 + ft, :], z[:, 8 + ft, :]
        col = lambda name, i=0: vec[:, l, VEC[name] + i:VEC[name] + i + 1]
        mid_l, dl, dcol = cols[:, 0:8], cols[:, 8:16], cols[:, 16:24]

        def start():
            n0 = nm + "_start"
            kraw, ksq, rs = e1, e2, e3
            s_sq, s_full, s_root, s_v, s_raw = (sem("c_start" + x, 1) for x in ("_sq", "_sum", "_root", "_vT", "_raw"))

            def pool(e):
                nc.gpsimd.tensor_scalar(kraw, k, col("k_k", ft), None, ALU.mult).then_inc(s_raw.h, 1)
                if ft == 0:
                    for m in (gt, hm, sm):
                        nc.gpsimd.memset(m.rearrange("p a b -> p (a b)"), 0.0)

            def act(e):
                e.wait_ge(s_raw.h, s_raw.at(1))
                nc.scalar.activation(ksq, kraw, ACT.Square).then_inc(s_sq.h, 1)
                e.wait_ge(s_full.h, s_full.at(1))
                nc.scalar.activation(rs, psum[:, 0, :], ACT.Sqrt).then_inc(s_root.h, 1)
                e.wait_ge(s_v.h, s_v.at(1))
                nc.scalar.activation(vtm.rearrange("p a b -> p (a b)"), psum[:, 1, :], ACT.Copy)

            def dve(e):
                e.wait_ge(s_root.h, s_root.at(1))
                link(e, nc.vector.tensor_scalar(rs, rs, 1e-12, None, ALU.max))
                link(e, nc.vector.reciprocal(rs, rs))
                nc.vector.tensor_tensor(kk, kraw, rs, ALU.mult)

            def pe(e):
                for tt in range(4):
                    i = nc.tensor.transpose(psum[:, 1, tt * P:(tt + 1) * P], v[:, tt * P:(tt + 1) * P], ident)
                    if tt == 3:
                        i.then_inc(s_v.h, 1)
                e.wait_ge(s_sq.h, s_sq.at(1))
                mm(psum[:, 0, :], blk, ksq, True, True).then_inc(s_full.h, 1)
            stages.append((n0, dict(pe=pe, act=act, dve=dve, pool=pool)))

        def prepare(d):
            n0 = f"{nm}_prep{d}"
            s_lo, s_th, s_mid, s_exp, s_op, s_tr, s_dl = (
                sem("c_prep" + x, n) for x, n in
                (("_lo", 2), ("_tanh", 2), ("_mid", 2), ("_exp", 3), ("_ops", 4), ("_tr", 3), ("_dl", 1)))
            reset = consts[:, R_RESET + d * T:R_RESET + (d + 1) * T]
            rows = slice(64 * d, 64 * d + 64)

            def pe(e):
                mm(psum[:, 0, :], small[rows, SC_DEC + ft * P:SC_DEC + (ft + 1) * P], z[rows, 12, :], True, True).then_inc(s_lo.h, 1)
                mm(psum[:, 1, :], small[rows, SC_AAA + ft * P:SC_AAA + (ft + 1) * P], z[rows, 13, :], True, True).then_inc(s_lo.h, 1)
                for n, (op, need) in enumerate(((al, 1), (be, 2), (ka, 3))):
                    e.wait_ge(s_op.h, s_op.at(need))
                    for tt in range(4):
                        i = nc.tensor.transpose(psum[:, 2 + n, tt * P:(tt + 1) * P], op[:, tt * P:(tt + 1) * P], ident)
                        if tt == 3:
                            i.then_inc(s_tr.h, 1)

            def act(e):
                for n, (dst, at) in enumerate(((lw, 0), (t2, 8))):
                    e.wait_ge(s_lo.h, s_lo.at(n + 1))
                    nc.scalar.activation(dst, psum[:, n, :], ACT.Tanh, scale=0.5,
                                              bias=drv[:, at + 4 * d + ft:at + 4 * d + ft + 1]).then_inc(s_th.h, 1)
                e.wait_ge(s_mid.h, s_mid.at(1))
                nc.scalar.activation(e2, L, ACT.Exp, scale=-1.0).then_inc(s_exp.h, 1)
                nc.scalar.activation(e1, L, ACT.Exp).then_inc(s_exp.h, 1)
                e.wait_ge(s_mid.h, s_mid.at(2))
                nc.scalar.activation(e3, e3, ACT.Exp).then_inc(s_exp.h, 1)
                e.wait_ge(s_dl.h, s_dl.at(1))
                nc.scalar.activation(dcol[:, :7], dl[:, :7], ACT.Exp)
                for n, dst in enumerate((av[:, :, :, 0, :], btm.rearrange("p a (b c) -> p a b c", b=2),
                                         ktm.rearrange("p a (b c) -> p a b c", b=2))):
                    e.wait_ge(s_tr.h, s_tr.at(n + 1))
                    nc.scalar.activation(dst, psum[:, 2 + n, :].rearrange("p (a b c) -> p a b c", a=4, b=2), ACT.Copy)

            def dve(e):
                e.wait_ge(s_th.h, s_th.at(1))
                link(e, nc.vector.tensor_scalar(lw, lw, -0.5 * DECAY, -0.5 * DECAY, ALU.mult, ALU.add))
                step = slice(None) if d == 0 else slice(None, None, -1)
                link(e, nc.vector.tensor_tensor_scan(L[:, step], reset[:, step], lw[:, step], 0.0, ALU.mult, ALU.add))
                L3 = L.rearrange("p (c t) -> p c t", t=CHUNK)
                link(e, nc.vector.tensor_scalar(mid_l.unsqueeze(2), L3[:, :, (CHUNK - 1) * (1 - d):(CHUNK - 1) * (1 - d) + 1],
                                             0.5, None, ALU.mult))
                nc.vector.tensor_tensor(L3, L3, mid_l.unsqueeze(2).broadcast_to([P, NCH, CHUNK]), ALU.subtract).then_inc(s_mid.h, 1)
                e.wait_ge(s_mid.h, s_mid.at(1))
                nc.vector.tensor_tensor(e3, L, lw, ALU.subtract).then_inc(s_mid.h, 1)
                if d == 0:
                    nc.vector.tensor_tensor(dl[:, 0:7], mid_l[:, 0:7], mid_l[:, 1:8], ALU.add).then_inc(s_dl.h, 1)
                else:
                    nc.vector.tensor_tensor(dl[:, 0:3], mid_l[:, 3:0:-1], mid_l[:, 2::-1], ALU.add)
                    nc.vector.tensor_tensor(dl[:, 3:4], mid_l[:, 0:1], mid_l[:, 7:8], ALU.add)
                    nc.vector.tensor_tensor(dl[:, 4:7], mid_l[:, 7:4:-1], mid_l[:, 6:3:-1], ALU.add).then_inc(s_dl.h, 1)
                e.wait_ge(s_th.h, s_th.at(2))
                nc.vector.tensor_scalar(ka, t2, drv[:, 16 + ft:17 + ft], drv[:, 20 + ft:21 + ft], ALU.mult, ALU.add)
                link(e, nc.vector.tensor_scalar(t2, t2, -0.5, -0.5, ALU.mult, ALU.add))
                link(e, nc.vector.tensor_tensor(ka, ka, k, ALU.mult))
                if d == 0:
                    nc.vector.tensor_copy(kssum, ka)
                else:
                    nc.vector.tensor_tensor(kssum, kssum, ka, ALU.add)
                nc.vector.tensor_tensor(be, t2, kk, ALU.mult)
                e.wait_ge(s_exp.h, s_exp.at(3))
                nc.vector.tensor_tensor(al, e3, kk, ALU.mult).then_inc(s_op.h, 1)
                e.wait_ge(s_op.h, s_op.at(1))
                nc.vector.tensor_tensor(be, be, e2, ALU.mult).then_inc(s_op.h, 1)
                nc.vector.tensor_tensor(ka, ka, e2, ALU.mult).then_inc(s_op.h, 1)
                nc.vector.tensor_tensor(rh, e1, r, ALU.mult).then_inc(s_op.h, 1)
            stages.append((n0, dict(pe=pe, act=act, dve=dve)))

        def chunks(d):
            n0 = f"{nm}_chunk{d}"
            at, other = d * R_DIR, (1 - d) * R_DIR
            strict, strict_t = (consts[:, o + R_STRICT:o + R_STRICT + P] for o in (at, other))
            incl = consts[:, at + R_INCL:at + R_INCL + P]
            level = [consts[:, at + R_LEVEL + j * P:at + R_LEVEL + (j + 1) * P] for j in range(LEVELS)]
            wide = lambda m: m.unsqueeze(1).broadcast_to([P, 4, P])
            four = lambda b: b.rearrange("p (a c) -> p a c", a=4)
            x_ready, m_ready = sem("c_inverse_step", 2 * LEVELS), sem("c_masked", 10)
            av_ready, wu_ready, m1v_full = sem("c_av", 2), sem("c_wu", 2), sem("c_m1v_full", 2)
            raw = Banks("c_raw", [0, 1, 2, 3], 10, free=m_ready)
            xt_full, b_full, xb_ready = (sem("c_" + n, t * (LEVELS - 1)) for n, t in
                                         (("xt_full", 2), ("b_full", 2), ("xb_ready", 4)))
            inv_c = Banks("c_join", [0, 1], 2 * (LEVELS - 1), free=x_ready)
            post_full = sem("c_post_full", 5)
            mats = (("N", be, al, strict), ("N_t", al, be, strict_t), ("M1", ka, al, strict), ("M3", ka, rh, incl),
                    ("M4", be, rh, incl))

            def pe(e):
                for hd in range(2):
                    for name, lo, hi, _ in mats:
                        ps, n_free = raw.take()
                        if n_free > 0:
                            e.wait_ge(raw.free.h, raw.free.at(n_free))
                        for tt in range(4):
                            s = slice(tt * P, (tt + 1) * P)
                            p = mm(ps[:, s], lo[64 * hd:64 * hd + 64, s], hi[64 * hd:64 * hd + 64, s], True, True)
                            if tt == 3:
                                p.then_inc(raw.full.h, 1)
                for hd in range(2):
                    e.wait_ge(m_ready.h, m_ready.at(5 * hd + 3))
                    for tt in range(4):
                        p = mm(psum[:, 6 + hd, tt * P:(tt + 1) * P], per_head[hd]["M1"][:, tt, :], vtm[:, tt, :], True, True)
                        if tt == 3:
                            p.then_inc(m1v_full.h, 1)
                e.wait_ge(av_ready.h, av_ready.at(2))
                e.wait_ge(m_ready.h, m_ready.at(10))
                for j in range(1, LEVELS):
                    for hd in range(2):
                        m = per_head[hd]
                        if 2 * (j - 1) + hd + 1 > 0:
                            e.wait_ge(x_ready.h, x_ready.at(2 * (j - 1) + hd + 1))
                        ps = psum[:, 4 + hd, :]
                        for tt in range(4):
                            i = nc.tensor.transpose(ps[:, tt * P:(tt + 1) * P], m["X"][:, tt, :], ident)
                            if tt == 3:
                                i.then_inc(xt_full.h, 1)
                        for tt in range(4):
                            p = mm(psum[:, 6 + hd, tt * P:(tt + 1) * P], m["N_t"][:, tt, :], m["X"][:, tt, :], True, True)
                            if tt == 3:
                                p.then_inc(b_full.h, 1)
                    for hd in range(2):
                        m = per_head[hd]
                        if 4 * (j - 1) + 2 * hd + 2 > 0:
                            e.wait_ge(xb_ready.h, xb_ready.at(4 * (j - 1) + 2 * hd + 2))
                        for tt in range(4):
                            p = mm(psum[:, hd, tt * P:(tt + 1) * P], m["X_t"][:, tt, :], m["B"][:, tt, :], True, True)
                            if tt == 3:
                                p.then_inc(inv_c.full.h, 1)
                for hd in range(2):
                    if 2 * (LEVELS - 1) + hd + 1 > 0:
                        e.wait_ge(x_ready.h, x_ready.at(2 * (LEVELS - 1) + hd + 1))
                    ps = psum[:, 2 + hd, :]
                    for tt in range(4):
                        p = mm(ps[:, tt * P:(tt + 1) * P], per_head[hd]["X"][:, tt, :], av[:, tt, hd, :, :].rearrange("p a b -> p (a b)"), True, True)
                        if tt == 3:
                            p.then_inc(post_full.h, 1)
                for c in range(2):
                    rows = slice(64 * c, 64 * c + 64)
                    ps = psum[:, 4 + c, :]
                    for hd in range(2):
                        o, f = slice(64 * hd, 64 * hd + 64), slice(64 * hd, 64 * hd + 64)
                        e.wait_ge(wu_ready.h, wu_ready.at(hd + 1))
                        for tt in range(4):
                            mm(ps[o, tt * 64:(tt + 1) * 64], wu[hd][rows, tt, 0:64], btm[rows, tt, f], True, True)
                        for tt in range(4):
                            q = slice(256 + tt * 64, 256 + (tt + 1) * 64)
                            mm(ps[o, q], ktm[rows, tt, f], vtm[rows, tt, f], True, False)
                            p = mm(ps[o, q], btm[rows, tt, f], wu[hd][rows, tt, 64:128], False, True)
                            if hd == 1 and tt == 3:
                                p.then_inc(post_full.h, 1)
                ps = psum[:, 2, :]
                for hd in range(2):
                    for tt in range(4):
                        p = mm(ps[64 * hd:64 * hd + 64, tt * P:(tt + 1) * P], wu[hd][:, tt, 0:64], per_head[hd]["M4"][:, tt, :], True, True)
                        if hd == 1 and tt == 3:
                            p.then_inc(post_full.h, 1)

            def act(e):
                for hd in range(2):
                    e.wait_ge(m1v_full.h, m1v_full.at(hd + 1))
                    nc.scalar.activation(av[:, :, hd, 1, :], four(psum[:, 6 + hd, :])[:, :, 64 * hd:64 * hd + 64],
                                              ACT.Copy).then_inc(av_ready.h, 1)
                for j in range(1, LEVELS):
                    for hd in range(2):
                        m = per_head[hd]
                        if 2 * (j - 1) + hd + 1 > 0:
                            e.wait_ge(xt_full.h, xt_full.at(2 * (j - 1) + hd + 1))
                        nc.scalar.activation(m["X_t"], four(psum[:, 4 + hd, :]), ACT.Copy).then_inc(xb_ready.h, 1)
                        if 2 * (j - 1) + hd + 1 > 0:
                            e.wait_ge(b_full.h, b_full.at(2 * (j - 1) + hd + 1))
                        nc.scalar.activation(m["B"], four(psum[:, 6 + hd, :]), ACT.Copy).then_inc(xb_ready.h, 1)
                for hd in range(2):
                    e.wait_ge(post_full.h, post_full.at(hd + 1))
                    nc.scalar.activation(wu[hd], four(psum[:, 2 + hd, :]), ACT.Copy).then_inc(wu_ready.h, 1)

            def dve(e):
                for hd in range(2):
                    for name, _, _, mask in mats:
                        ps, n_full = raw.arrived()
                        e.wait_ge(raw.full.h, raw.full.at(n_full))
                        nc.vector.tensor_tensor(per_head[hd][name], four(ps), wide(mask), ALU.mult).then_inc(m_ready.h, 1)
                        if name == "N":
                            e.wait_ge(m_ready.h, m_ready.at(5 * hd + 1))
                            link(e, nc.vector.tensor_tensor(per_head[hd]["X"], per_head[hd]["N"], wide(level[0]), ALU.mult))
                            nc.vector.tensor_tensor(per_head[hd]["X"], per_head[hd]["X"], wide(ident), ALU.add).then_inc(x_ready.h, 1)
                for j in range(1, LEVELS):
                    for hd in range(2):
                        ps, n_full = inv_c.arrived()
                        e.wait_ge(inv_c.full.h, inv_c.full.at(n_full))
                        nc.vector.copy_predicated(per_head[hd]["X"], wide(level[j].bitcast(u32)), four(ps)).then_inc(x_ready.h, 1)
                D3 = lambda m, c: m[:, :, :].rearrange("p (t c) f -> p t c f", c=2)[:, :, c, :]
                for c in range(2):
                    e.wait_ge(post_full.h, post_full.at(3 + c))
                    ps = psum[:, 4 + c, :]
                    for hd in range(2):
                        o = slice(64 * hd, 64 * hd + 64)
                        eye = ident[o, o].unsqueeze(1).broadcast_to([64, 4, 64])
                        nc.vector.tensor_tensor(D3(gt, c)[o, :, o], ps[o, 0:256].rearrange("p (a b) -> p a b", a=4),
                                                     eye, ALU.add)
                        nc.vector.tensor_copy(D3(hm, c)[o, :, o], ps[o, 256:512].rearrange("p (a b) -> p a b", a=4))
                e.wait_ge(post_full.h, post_full.at(5))
                nc.vector.tensor_tensor(rmat, psum[:, 2, :], rh, ALU.add)
            stages.append((n0, dict(pe=pe, act=act, dve=dve)))

        def scan(d):
            n0 = f"{nm}_scan{d}"
            order = list(range(NCH)) if d == 0 else [3, 2, 1, 0, 7, 6, 5, 4]
            s_state, s_prod, s_y = sem("c_state", NCH - 1), sem("c_product", NCH - 2), sem("c_y", 1)
            hm_scaled = sem("c_hm_scaled", 1)

            def pe(e):
                ps = psum[:, 7, :]
                for hd in range(2):
                    m = per_head[hd]
                    o = slice(64 * hd, 64 * hd + 64)
                    for tt in range(4):
                        q = slice(tt * P, (tt + 1) * P)
                        mm(ps[o, q], vtm[:, tt, o], m["M3"][:, tt, :], tt == 0, False, check=True)
                        mm(ps[o, q], wu[hd][:, tt, 64:128], m["M4"][:, tt, :], False, False, check=True)
                for i in range(1, NCH):
                    e.wait_ge(s_state.h, s_state.at(i))
                    c = order[i]
                    if i < NCH - 1:
                        mm(psum[:, i % 2, :P], gt[:, c, :], sm[:, c, :], True, True).then_inc(s_prod.h, 1)
                    q = slice(c * CHUNK, (c + 1) * CHUNK)
                    p = mm(ps[:, q], sm[:, c, :], rmat[:, q], False, i == NCH - 1, check=True)
                    if i == NCH - 1:
                        p.then_inc(s_y.h, 1)

            def dve(e):
                for i in range(NCH - 1):
                    c, nxt = order[i], order[i + 1]
                    if i == 0:
                        nc.vector.tensor_scalar(sm[:, nxt, :], hm[:, c, :], dcol[:, i:i + 1], None, ALU.mult).then_inc(s_state.h, 1)
                    else:
                        p = nc.vector.tensor_scalar(hm[:, c, :], hm[:, c, :], dcol[:, i:i + 1], None, ALU.mult)
                        if i == NCH - 2:
                            p.then_inc(hm_scaled.h, 1)
                for i in range(1, NCH - 1):
                    c, nxt = order[i], order[i + 1]
                    if i == 1:
                        e.wait_ge(hm_scaled.h, hm_scaled.at(1))
                    e.wait_ge(s_prod.h, s_prod.at(i))
                    nc.vector.scalar_tensor_tensor(sm[:, nxt, :], psum[:, i % 2, :P], dcol[:, i:i + 1], hm[:, c, :],
                                                        ALU.mult, ALU.add).then_inc(s_state.h, 1)
                e.wait_ge(s_y.h, s_y.at(1))
                if d == 0:
                    nc.vector.tensor_copy(o_c[:, ft, :], psum[:, 7, :])
                else:
                    nc.vector.tensor_tensor(o_c[:, ft, :], o_c[:, ft, :], psum[:, 7, :], ALU.add)
            stages.append((n0, dict(pe=pe, dve=dve)))

        def finish():
            n0 = nm + "_out"
            y, yc, sq, bon, rs = o_c[:, ft, :], al, be, ka, rh
            s1, s2, s3, s4, s5, s6 = (sem("c_out" + x, 1) for x in
                                      ("_mean", "_centred", "_squared", "_var", "_std", "_bonus"))
            s7 = sem("c_out_gate", 2)

            def pe(e):
                mm(psum[:, 0, :], blk, y, True, True).then_inc(s1.h, 1)
                mm(psum[:, 1, :], small[:, SC_GATE + ft * P:SC_GATE + (ft + 1) * P], z[:, 14, :], True, True).then_inc(s7.h, 1)
                e.wait_ge(s6.h, s6.at(1))
                mm(psum[:, 3, :], blk, bon, True, True).then_inc(s7.h, 1)
                e.wait_ge(s3.h, s3.at(1))
                mm(psum[:, 2, :], blk, sq, True, True).then_inc(s4.h, 1)

            def act(e):
                e.wait_ge(s2.h, s2.at(1))
                nc.scalar.activation(sq, yc, ACT.Square).then_inc(s3.h, 1)
                e.wait_ge(s4.h, s4.at(1))
                nc.scalar.activation(rs, psum[:, 2, :], ACT.Sqrt, bias=gn_eps, scale=1.0 / HD).then_inc(s5.h, 1)

            def pool(e):
                link(e, nc.gpsimd.tensor_scalar(e1, kssum, col("r_k", ft), None, ALU.mult))
                nc.gpsimd.tensor_tensor(bon, r, e1, ALU.mult).then_inc(s6.h, 1)

            def dve(e):
                e.wait_ge(s1.h, s1.at(1))
                nc.vector.scalar_tensor_tensor(yc, psum[:, 0, :], -1.0 / HD, y, ALU.mult, ALU.add).then_inc(s2.h, 1)
                e.wait_ge(s7.h, s7.at(2))
                nc.vector.tensor_tensor(e2, psum[:, 3, :], v, ALU.mult)
                e.wait_ge(s5.h, s5.at(1))
                link(e, nc.vector.reciprocal(rs, rs))
                link(e, nc.vector.tensor_tensor(yc, yc, rs, ALU.mult))
                link(e, nc.vector.tensor_scalar(yc, yc, col("gn_w", ft), col("gn_b", ft), ALU.mult, ALU.add))
                link(e, nc.vector.tensor_tensor(yc, yc, e2, ALU.add))
                nc.vector.tensor_tensor(y, yc, psum[:, 1, :], ALU.mult)
            stages.append((n0, dict(pe=pe, act=act, dve=dve, pool=pool)))

        start()
        for d in range(2):
            prepare(d)
            chunks(d)
            scan(d)
        finish()

    def stage_merge(l, tok):
        nm = f"merge{l}"
        n = tok.stop - tok.start
        take, pos = carver()
        y, gate, part = take(KT, T), take(2, T), take(2, T)
        gates, prods, outs = (Banks("merge_gates", [0, 1, 2], 4 * KT), Banks("merge_products", [3, 4, 5], 4 * KT),
                               Banks("merge_outs", [6, 7], KT))
        y_ready = sem("merge_y_ready", KT)
        gate_used = prods.free

        def pe(e):
            for m in range(KT):
                for i in (0, 2):
                    for g in range(2):
                        panel_fm(e, gates, h, tok)
                    w, slot_in, n_in = stream.take()
                    e.wait_ge(slot_in.h, n_in)
                    for g in range(2):
                        ps, n_free = prods.take()
                        if n_free > 0:
                            e.wait_ge(prods.free.h, prods.free.at(n_free))
                        for k in range(4):
                            p = mm(ps[:, :n], w[:, 4 * g + k, :], branch[i + g][:, k, tok], k == 0, k == 3)
                            if g == 0 and k == 0:
                                p.then_inc(panels_begun.h, 1)
                        p.then_inc(prods.full.h, 1)
            for m in range(KT):
                if m == 0:
                    e.wait_ge(y_ready.h, y_ready.at(KT))
                panel_fm(e, outs, y, tok)

        def act(e):
            for n_ in range(4 * KT):
                ps, n_full = gates.arrived()
                e.wait_ge(gates.full.h, gates.full.at(n_full))
                if n_ - 1 > 0:
                    e.wait_ge(gate_used.h, gate_used.at(n_ - 1))
                nc.scalar.activation(gate[:, n_ % 2, :n], ps[:, :n], ACT.Tanh, scale=0.5).then_inc(gates.free.h, 1)

        def dve(e):
            for m in range(KT):
                for i in range(4):
                    n_ = 4 * m + i
                    g = gate[:, n_ % 2, :n]
                    e.wait_ge(gates.free.h, gates.free.at(n_ + 1))
                    link(e, nc.vector.tensor_scalar(g, g, 1.0, 0.5, ALU.add, ALU.mult))
                    ps, n_full = prods.arrived()
                    e.wait_ge(prods.full.h, prods.full.at(n_full))
                    dst = y[:, m, tok] if i == 0 else part[:, n_ % 2, :n]
                    nc.vector.tensor_tensor(dst, ps[:, :n], g, ALU.mult).then_inc(prods.free.h, 1)
                    if i:
                        e.wait_ge(prods.free.h, prods.free.at(n_ + 1))
                        p = nc.vector.tensor_tensor(y[:, m, tok], y[:, m, tok], dst, ALU.add)
                        if i == 3:
                            p.then_inc(y_ready.h, 1)
            residual(e, outs, l, 16, tok)
        stages.append((nm, dict(pe=pe, act=act, dve=dve)))

    def residual(e, outs, l, j0, tok):
        for m in range(KT):
            ps, n_full = outs.arrived()
            e.wait_ge(outs.full.h, outs.full.at(n_full))
            segs = [(s, seg) for s, seg in ((0, slice(0, CTX)), (1, mid)) if seg.start >= tok.start]
            for s, seg in segs:
                src = ps[:, seg.start - tok.start:seg.stop - tok.start]
                p = nc.vector.scalar_tensor_tensor(x[:, m, seg], src, mod[:, j0 + m, s:s + 1], x[:, m, seg],
                                                   ALU.mult, ALU.add)
            p.then_inc(outs.free.h, 1)

    def stage_mlp(l, tok):
        nm = f"mlp{l}"
        n = tok.stop - tok.start
        take, pos = carver()
        hid, relu = take(32, T), take(2, T)
        ups, outs = Banks("mlp_ups", [0, 1, 2, 3], N_UP), Banks("mlp_outs", [4, 5, 6, 7], KT)
        hid_ready = sem("mlp_hidden", N_UP)

        def pe(e):
            for j in range(N_UP):
                panel_fm(e, ups, h, tok)
            for m in range(KT):
                ps, n_free = outs.take()
                if n_free > 0:
                    e.wait_ge(outs.free.h, outs.free.at(n_free))
                for q in range(4):
                    w, slot_in, n_in = stream.take()
                    e.wait_ge(slot_in.h, n_in)
                    for k in range(KT):
                        if m == 0:
                            e.wait_ge(hid_ready.h, hid_ready.at(8 * q + k + 1))
                        p = mm(ps[:, :n], w[:, k, :], hid[:, 8 * q + k, tok], q == 0 and k == 0, q == 3 and k == 7)
                        if k == 0:
                            p.then_inc(panels_begun.h, 1)
                p.then_inc(outs.full.h, 1)

        def act(e):
            for j in range(N_UP):
                ps, n_full = ups.arrived()
                e.wait_ge(ups.full.h, ups.full.at(n_full))
                if j - 1 > 0:
                    e.wait_ge(hid_ready.h, hid_ready.at(j - 1))
                nc.scalar.activation(relu[:, j % 2, :n], ps[:, :n], ACT.Relu).then_inc(ups.free.h, 1)

        def dve(e):
            for j in range(N_UP):
                e.wait_ge(ups.free.h, ups.free.at(j + 1))
                r = relu[:, j % 2, :n]
                nc.vector.tensor_tensor(hid[:, j, tok], r, r, ALU.mult).then_inc(hid_ready.h, 1)
            residual(e, outs, l, 40, tok)
        stages.append((nm, dict(pe=pe, act=act, dve=dve)))

    full_row, lat_row = slice(0, T), mid
    for l in range(DEPTH):
        rows = full_row if l < DEPTH - 1 else lat_row
        stage_ada(l)
        stage_norm(f"norm1_{l}", l, 0, full_row)
        stage_c(l)
        stage_a(l)
        stage_b(l)
        stage_d(l)
        stage_merge(l, rows)
        stage_norm(f"norm2_{l}", l, 1, rows)
        stage_mlp(l, rows)
    stage_norm("final", DEPTH - 1, 0, lat_row, final=True)

    stage_end = sem("stage_end")
    ENGINES = 4

    def run(eng, key):
        own[id(eng)] = [sem(key + "_steps").h, 0]
        for i, (name, parts) in enumerate(stages):
            if key in parts:
                parts[key](eng)
            eng.drain().then_inc(stage_end.h, 1)
            eng.wait_ge(stage_end.h, ENGINES * (i + 1))

    with ctx, nc.Block() as block:
        @block.tensor
        def _(eng):
            run(eng, "pe")

        @block.scalar
        def _(eng):
            run(eng, "act")

        @block.vector
        def _(eng):
            run(eng, "dve")

        @block.gpsimd
        def _(eng):
            run(eng, "pool")

        @block.sync
        def _(eng):
            n_all = stream.n
            for n in range(n_all):
                slot = n % SLOTS
                if n >= SLOTS:
                    eng.wait_ge(panels_begun.h, n - SLOTS + 2)
                eng.dma_start(ring[:, slot, :, :], panels[n // N_PANELS, n % N_PANELS].rearrange("p (k m) -> p k m", k=KT)).then_inc(sem(f"panel_in_{slot}").h, 16)
            eng.wait_ge(stage_end.h, ENGINES * len(stages))
            eng.dma_start(out_t.rearrange("(k p) t -> p k t", p=P), h[:, :, mid]).then_inc(sem("stored").h, 16)
            eng.wait_ge(sem("stored").h, 16)


def kernel(x, c, ctx, c_ctx, w_ada, b_ada, g_norm1, g_norm2, w_in, a_q_gain, a_k_gain, b_q_gain, b_kv_gain,
           b_w_q_up, b_w_kv_up, c_mu, c_w0, c_w_decay, c_a0, c_w_aaa, c_w_gate, c_k_k, c_k_a, c_r_k,
           c_gn_w, c_gn_b, d_rel_bias, w_branch, w_out, w_mlp1, w_mlp2, g_final):
    import concourse.bacc as bacc
    from concourse.bass_utils import run_bass_kernel_spmd

    a = {k: np.asarray(v) for k, v in locals().items() if isinstance(v, np.ndarray) or hasattr(v, "dtype")}
    g, t, r = _shape_constants()
    sb_, sc_ = _lay_small(a["b_w_q_up"], a["b_w_kv_up"], a["c_w_decay"], a["c_w_aaa"], a["c_w_gate"])
    cc = np.stack([a["c_ctx"].reshape(KT, P), a["c"].reshape(KT, P)], -1)
    arrays = {
        "x_t": np.ascontiguousarray(np.concatenate([a["ctx"][0].T, a["x"][0].T], 1)),
        "c_cols": np.ascontiguousarray(cc.transpose(1, 0, 2)).reshape(P, 2 * KT),
        "panels": _lay_panels(a["w_ada"], a["w_in"], a["w_branch"], a["w_out"], a["w_mlp1"], a["w_mlp2"]),
        "vectors": _lay_vectors(a),
        "small_b": sb_, "small_c": sc_,
        "bias_d": _lay_bias(a["d_rel_bias"]),
        "const_g": g, "const_t": t, "const_r": r,
    }
    nc = bacc.Bacc("TRN2", target_bir_lowering=False, num_devices=1)
    args = [nc.dram_tensor(n, v.shape, mybir.dt.from_np(v.dtype), kind="ExternalInput").ap() for n, v in arrays.items()]
    out = nc.dram_tensor("out_t", (D_MODEL, SEQ), mybir.dt.float32, kind="ExternalOutput").ap()
    build(nc, *args, out)
    res = run_bass_kernel_spmd(nc, [arrays], core_ids=[0])
    return np.ascontiguousarray(np.asarray(res.results[0]["out_t"]).T)[None]
```
